# Optimizing a Trainium2 kernel written in Bass

```python
import jax, jax.numpy as jnp
from jax import lax
import numpy as np

D_MODEL = 1024
BATCH = 1
SEQ = 256
DEPTH = 2

POOL_WINDOWS = (2, 4, 8, 16)
N_POOL_GROUPS = len(POOL_WINDOWS)
POOL_WIDTH = D_MODEL // 2
POOL_GROUP = POOL_WIDTH // N_POOL_GROUPS
POOL_OUT_GROUP = D_MODEL // N_POOL_GROUPS
ATTN_HEADS = 8
HEAD_DIM = 64
ATTN_WIDTH = ATTN_HEADS * HEAD_DIM
MOBA_BLOCK = 256
MOBA_TOPK = 3
Q_CHUNK = 16
N_BRANCHES = 2
IN_WIDTH = POOL_WIDTH + 3 * ATTN_WIDTH + N_BRANCHES * D_MODEL
PEER_HEADS = 8
PEER_NKEYS = 128
PEER_EXPERTS = PEER_NKEYS * PEER_NKEYS
PEER_QDIM = 256
PEER_HALF = PEER_QDIM // 2
PEER_TOPK = 16
TOKEN_CHUNK = 128
EPS = 1e-6

kernel_name = "hybrid_pool_moba_peer_trunk"

def rmsnorm(x, g):
    xf = x.astype(jnp.float32)
    y = xf * lax.rsqrt(jnp.mean(xf * xf, axis=-1, keepdims=True) + EPS)
    return (y * g.astype(jnp.float32)).astype(x.dtype)

def alibi_slopes(n_heads):
    return jnp.asarray([2.0 ** (-8.0 * (h + 1) / n_heads) for h in range(n_heads)], jnp.float32)

def pool_mixer(p, w_pool, pool_scale):
    B_, S_, _ = p.shape
    pf = p.astype(jnp.float32)
    c = jnp.pad(jnp.cumsum(pf, axis=1), ((0, 0), (1, 0), (0, 0)))
    pos = jnp.arange(S_)
    outs = []
    for gi, w in enumerate(POOL_WINDOWS):
        cg = c[..., gi * POOL_GROUP:(gi + 1) * POOL_GROUP]
        start = jnp.maximum(pos + 1 - w, 0)
        cnt = (pos + 1 - start).astype(jnp.float32)
        win_mean = (cg[:, 1:] - jnp.take(cg, start, axis=1)) / cnt[None, :, None]
        outs.append(win_mean - pf[..., gi * POOL_GROUP:(gi + 1) * POOL_GROUP])
    m = jnp.stack(outs, axis=2)
    y = jnp.einsum('bsgc,gco->bsgo', m, w_pool.astype(jnp.float32)).reshape(B_, S_, D_MODEL)
    return (y * pool_scale.astype(jnp.float32)).astype(p.dtype)

def moba_attention(q, k, v):
    B_, H_, S_, dh = q.shape
    n_blk = -(-S_ // MOBA_BLOCK)
    pad = n_blk * MOBA_BLOCK - S_
    kp = jnp.pad(k, ((0, 0), (0, 0), (0, pad), (0, 0)))
    vp = jnp.pad(v, ((0, 0), (0, 0), (0, pad), (0, 0)))
    k_blocks = kp.reshape(B_, H_, n_blk, MOBA_BLOCK, dh)
    v_blocks = vp.reshape(B_, H_, n_blk, MOBA_BLOCK, dh)
    k_mean = jnp.mean(k_blocks.astype(jnp.float32), axis=3)
    top = min(MOBA_TOPK, n_blk)
    slopes = alibi_slopes(H_)
    scale = dh ** -0.5
    b_ix = jnp.arange(B_)[:, None, None, None]
    h_ix = jnp.arange(H_)[None, :, None, None]
    blk_ids = jnp.arange(n_blk)
    offs = jnp.arange(MOBA_BLOCK)

    def chunk(ci):
        t0 = ci * Q_CHUNK
        qc = lax.dynamic_slice_in_dim(q, t0, Q_CHUNK, axis=2).astype(jnp.float32)
        t = t0 + jnp.arange(Q_CHUNK)
        own = t0 // MOBA_BLOCK
        bscore = jnp.einsum('bhcd,bhnd->bhcn', qc, k_mean)
        bscore = jnp.where(blk_ids < own, bscore, -jnp.inf)
        _, sel = lax.top_k(bscore, top)
        sel_ok = sel < own
        kg = k_blocks[b_ix, h_ix, sel].astype(jnp.float32)
        vg = v_blocks[b_ix, h_ix, sel].astype(jnp.float32)
        s_sel = jnp.einsum('bhcd,bhcjkd->bhcjk', qc, kg) * scale
        dist_sel = t[None, None, :, None, None] - (sel[..., None] * MOBA_BLOCK + offs)
        s_sel = s_sel - slopes[None, :, None, None, None] * dist_sel
        s_sel = jnp.where(sel_ok[..., None], s_sel, -jnp.inf)
        k_own = lax.dynamic_slice_in_dim(kp, own * MOBA_BLOCK, MOBA_BLOCK, axis=2).astype(jnp.float32)
        v_own = lax.dynamic_slice_in_dim(vp, own * MOBA_BLOCK, MOBA_BLOCK, axis=2).astype(jnp.float32)
        dist_own = t[:, None] - (own * MOBA_BLOCK + offs)[None, :]
        s_own = jnp.einsum('bhcd,bhkd->bhck', qc, k_own) * scale
        s_own = s_own - slopes[None, :, None, None] * dist_own
        s_own = jnp.where(dist_own >= 0, s_own, -jnp.inf)
        s_all = jnp.concatenate([s_sel.reshape(B_, H_, Q_CHUNK, top * MOBA_BLOCK), s_own], axis=-1)
        pr = jax.nn.softmax(s_all, axis=-1)
        p_sel = pr[..., :top * MOBA_BLOCK].reshape(B_, H_, Q_CHUNK, top, MOBA_BLOCK)
        p_own = pr[..., top * MOBA_BLOCK:]
        o = (jnp.einsum('bhcjk,bhcjkd->bhcd', p_sel, vg)
             + jnp.einsum('bhck,bhkd->bhcd', p_own, v_own))
        return o.astype(q.dtype)

    out = lax.map(chunk, jnp.arange(S_ // Q_CHUNK))
    return out.transpose(1, 2, 0, 3, 4).reshape(B_, H_, S_, dh)

def peer_ffn(x, w_q, sub_keys, u, v):
    B_, S_, D_ = x.shape
    xt = x.reshape((B_ * S_) // TOKEN_CHUNK, TOKEN_CHUNK, D_)

    def chunk(xc):
        q = (xc @ w_q).reshape(TOKEN_CHUNK, PEER_HEADS, 2, PEER_HALF).astype(jnp.float32)
        s = jnp.einsum('thpd,pkd->thpk', q, sub_keys.astype(jnp.float32))
        sv, si = lax.top_k(s, PEER_TOPK)
        cand = sv[:, :, 0, :, None] + sv[:, :, 1, None, :]
        cand_id = si[:, :, 0, :, None] * PEER_NKEYS + si[:, :, 1, None, :]
        cv, ci = lax.top_k(cand.reshape(TOKEN_CHUNK, PEER_HEADS, PEER_TOPK * PEER_TOPK), PEER_TOPK)
        eid = jnp.take_along_axis(cand_id.reshape(TOKEN_CHUNK, PEER_HEADS, PEER_TOPK * PEER_TOPK), ci, axis=-1)
        g = jax.nn.softmax(cv, axis=-1)
        ug = u[eid].astype(jnp.float32)
        vg = v[eid].astype(jnp.float32)
        act = jax.nn.gelu(jnp.einsum('thkd,td->thk', ug, xc.astype(jnp.float32)))
        y = jnp.einsum('thk,thkd->td', g * act, vg)
        return y.astype(x.dtype)

    return lax.map(chunk, xt).reshape(B_, S_, D_)

def hybrid_layer(x, g_mix, w_in, w_pool, pool_scale, w_attn_up, w_out, g_ffn, w_peer_q, peer_keys, peer_u, peer_v):
    B_, S_, _ = x.shape
    h = rmsnorm(x, g_mix)
    z = h @ w_in
    o1 = POOL_WIDTH
    o2 = o1 + ATTN_WIDTH
    o3 = o2 + ATTN_WIDTH
    o4 = o3 + ATTN_WIDTH
    p, q, k, v, gl = z[..., :o1], z[..., o1:o2], z[..., o2:o3], z[..., o3:o4], z[..., o4:]
    branch_a = pool_mixer(p, w_pool, pool_scale)
    to_heads = lambda t: t.reshape(B_, S_, ATTN_HEADS, HEAD_DIM).transpose(0, 2, 1, 3)
    o = moba_attention(to_heads(q), to_heads(k), to_heads(v))
    branch_b = o.transpose(0, 2, 1, 3).reshape(B_, S_, ATTN_WIDTH) @ w_attn_up
    gates = jax.nn.sigmoid(gl.astype(jnp.float32)).astype(x.dtype)
    merged = gates[..., :D_MODEL] * branch_a + gates[..., D_MODEL:] * branch_b
    x = x + merged @ w_out
    x = x + peer_ffn(rmsnorm(x, g_ffn), w_peer_q, peer_keys, peer_u, peer_v)
    return x

def setup_inputs(seed: int = 0) -> dict:
    key = jax.random.key(seed)
    ks = jax.random.split(key, 14)
    f = jnp.float32
    nrm = lambda k_, shape, s: jax.random.normal(k_, shape, f) * s
    return {
        "x": nrm(ks[0], (BATCH, SEQ, D_MODEL), 1.0),
        "mix_norm": 1.0 + nrm(ks[1], (DEPTH, D_MODEL), 0.02),
        "w_in": nrm(ks[2], (DEPTH, D_MODEL, IN_WIDTH), D_MODEL ** -0.5),
        "w_pool": nrm(ks[3], (DEPTH, N_POOL_GROUPS, POOL_GROUP, POOL_OUT_GROUP), POOL_GROUP ** -0.5),
        "pool_scale": 1.0 + nrm(ks[4], (DEPTH, D_MODEL), 0.02),
        "w_attn_up": nrm(ks[5], (DEPTH, ATTN_WIDTH, D_MODEL), ATTN_WIDTH ** -0.5),
        "w_out": nrm(ks[6], (DEPTH, D_MODEL, D_MODEL), D_MODEL ** -0.5),
        "ffn_norm": 1.0 + nrm(ks[7], (DEPTH, D_MODEL), 0.02),
        "peer_wq": nrm(ks[8], (DEPTH, D_MODEL, PEER_HEADS * PEER_QDIM), D_MODEL ** -0.5),
        "peer_keys": nrm(ks[9], (DEPTH, 2, PEER_NKEYS, PEER_HALF), PEER_HALF ** -0.5),
        "peer_u": nrm(ks[10], (DEPTH, PEER_EXPERTS, D_MODEL), D_MODEL ** -0.5),
        "peer_v": nrm(ks[11], (DEPTH, PEER_EXPERTS, D_MODEL), PEER_HEADS ** -0.5),
        "final_norm": 1.0 + nrm(ks[12], (D_MODEL,), 0.02),
    }

def reference(x, mix_norm, w_in, w_pool, pool_scale, w_attn_up, w_out, ffn_norm, peer_wq, peer_keys, peer_u, peer_v, final_norm):
    for l in range(DEPTH):
        x = hybrid_layer(x, mix_norm[l], w_in[l], w_pool[l], pool_scale[l], w_attn_up[l], w_out[l],
                         ffn_norm[l], peer_wq[l], peer_keys[l], peer_u[l], peer_v[l])
    return rmsnorm(x, final_norm)


_drawn_inputs = setup_inputs


def setup_inputs(seed=0):
    import zlib

    import numpy as np

    out = dict(_drawn_inputs(seed))
    spreads = {}
    factors = {}
    for name, (base, spread) in spreads.items():
        noise = np.random.default_rng([zlib.crc32(name.encode()), seed]).standard_normal(out[name].shape)
        drawn = base * np.exp(spread * noise) if base else spread * noise
        out[name] = __import__('jax').numpy.asarray(drawn.astype(out[name].dtype))
    for name, factor in factors.items():
        out[name] = (out[name] * factor).astype(out[name].dtype)
    return out
```

```python
from contextlib import ExitStack

import numpy as np
import concourse.bass as bass
from concourse import mybir

F32 = mybir.dt.float32
U32 = mybir.dt.uint32
ALU = mybir.AluOpType
ACT = mybir.ActivationFunctionType
AX = mybir.AxisListType

P = 128
S = 256
NT = S // P
D = 1024
KC = D // P
HEADS, DH = 8, 64
WINDOWS = (2, 4, 8, 16)
NG = len(WINDOWS)
GOUT = D // NG
AW = HEADS * DH
NA = AW // P
PH, NK, TOPK = 8, 128, 16
NHP = 2 * PH
HK = PH * TOPK
EXPERTS = NK * NK
EPS = 1e-6
LOWEST = -3.0e38
MASKED = -1.0e30

CW = 512
IN_CHUNKS, OUT_CHUNKS, PQ_CHUNKS = 8, 2, 4
W_SLOTS = 3
RING = 16
HALF = RING // 2
KEYS_ALL = P + 2 * P

C_ID = 0
C_IOTA = C_ID + P
C_DIST = C_IOTA + TOPK
C_BAND = C_DIST + KEYS_ALL
C_ALL = C_BAND + NG * NT * S


def constants():
    c = np.zeros((P, C_ALL), np.float32)
    c[:, C_ID:C_ID + P] = np.eye(P, dtype=np.float32)
    c[:, C_IOTA:C_IOTA + TOPK] = np.arange(TOPK)
    q, k = np.arange(P)[:, None], np.arange(S)[None, :]
    dist = c[:, C_DIST:C_DIST + KEYS_ALL]
    dist[:, :P] = np.where(k[:, :P] <= q, k[:, :P] - q, MASKED)
    dist[:, P:] = np.where(k <= q + P, k - q - P, MASKED)
    band = c[:, C_BAND:].reshape(P, NG, NT, S)
    t = np.arange(S)
    for g, w in enumerate(WINDOWS):
        src = np.arange(S)[:, None]
        inside = (src <= t) & (src > t - w)
        m = np.where(inside, 1.0 / np.minimum(t + 1, w), 0.0) - (src == t)
        band[:, g] = m.reshape(NT, P, S).transpose(1, 0, 2)
    return c


def build(nc, consts, x, mix_norm, w_in, w_pool, pool_scale, w_attn_up, w_out, ffn_norm, peer_wq,
          peer_keys, peer_u, peer_v, final_norm, out):
    depth = mix_norm.shape[0]
    u_rows = peer_u.rearrange("l n d -> (l n) d")
    v_rows = peer_v.rearrange("l n d -> (l n) d")

    with ExitStack() as ctx:
        def sb(name, shape, dt=F32):
            return ctx.enter_context(nc.sbuf_tensor(name, shape, dt))

        sems = []

        def sem(name):
            s = ctx.enter_context(nc.semaphore(name))
            sems.append(s)
            return s

        cst = sb("cst", [P, C_ALL])
        ident = cst[:, C_ID:C_ID + P]
        iota16 = cst[:, C_IOTA:C_IOTA + TOPK]
        dist = cst[:, C_DIST:C_DIST + KEYS_ALL]
        band = cst[:, C_BAND:].rearrange("p (g a t) -> p g a t", g=NG, a=NT)

        xs = sb("xs", [P, NT, D])
        h = sb("h", [P, NT, D])
        hT = sb("hT", [P, KC, S])
        gmix = sb("gmix", [P, D])
        gffn = sb("gffn", [P, D])
        pscale = sb("pscale", [P, D])
        wpool = sb("wpool", [P, NG, GOUT])
        keys = sb("keys", [P, 2, P])
        keysT = sb("keysT", [P, 2, NK])
        wring = sb("wring", [P, W_SLOTS, KC, CW])
        acc = sb("acc", [P, 2, D])
        cand = sb("cand", [P, PH, TOPK * TOPK])
        tmp = cand[:, 0:4, :].rearrange("p (a b) n -> p a (b n)", a=2)
        sv = sb("sv", [P, NHP, TOPK])
        si = sb("si", [P, NHP, TOPK], U32)
        sif = sb("sif", [P, NHP, TOPK])
        cv = sb("cv", [P, PH, TOPK])
        ci = sb("ci", [P, HK], U32)
        cab = sb("cab", [P, 2, HK], U32)
        cabf = sb("cabf", [P, 2, HK])
        picked = sb("picked", [P, 2, HK])
        gsum = sb("gsum", [P, PH])
        prob = sb("prob", [P, NT, HK])
        expert = sb("expert", [P, NT, HK], U32)
        stage = sb("stage", [P, 2, HALF], U32)
        dots = sb("dots", [P, HK])
        g1 = sb("g1", [P, HK])
        g2 = sb("g2", [P, HK])
        wgt = sb("wgt", [P, HK])
        base = sb("base", [P, 1])
        stat = sb("stat", [P, 3, NT])
        smax = sb("smax", [P, HEADS, NT])
        ssum = sb("ssum", [P, HEADS, NT])
        srec = sb("srec", [P, HEADS, NT])

        shared = sb("shared", [P, NT * NHP * NK])
        wup = shared[:, 0:NA * D].rearrange("p (c n) -> p c n", c=NA)
        score = shared[:, :].rearrange("p (t a k) -> p t a k", t=NT, a=NHP)

        arena = sb("arena", [P, RING * D])
        ring = arena[:, :].rearrange("p (r d) -> p r d", r=RING)
        at = [0]

        def part(n):
            at[0] += n
            return arena[:, at[0] - n:at[0]]

        gates = part(NT * 2 * D).rearrange("p (t n) -> p t n", t=NT)
        soft = part(HEADS * KEYS_ALL).rearrange("p (h n) -> p h n", h=HEADS)
        softT = part(HEADS * KEYS_ALL).rearrange("p (h n) -> p h n", h=HEADS)
        p_sb = part(NT * CW).rearrange("p (t n) -> p t n", t=NT)
        v_sb = part(NT * CW).rearrange("p (t n) -> p t n", t=NT)
        qT = part(NA * S).rearrange("p (c n) -> p c n", c=NA)
        kT = part(NA * S).rearrange("p (c n) -> p c n", c=NA)
        mT = part(NG * S).rearrange("p (c n) -> p c n", c=NG)
        oT = part(NA * S).rearrange("p (c n) -> p c n", c=NA)
        pqT = arena[:, 0:NHP * S].rearrange("p (a n) -> p a n", a=NHP)

        abank = [ctx.enter_context(nc.psum_tensor(f"abank{i}", [P, CW], F32)) for i in range(4)]
        vbank = [ctx.enter_context(nc.psum_tensor(f"vbank{i}", [P, CW], F32)) for i in range(4)]

        x_in = sem("x_in")
        cst_in = sem("cst_in")
        small_in = sem("small_in")
        w_landed = [sem(f"w_landed{i}") for i in range(W_SLOTS)]
        w_used = sem("w_used")
        a_full, a_done = sem("a_full"), sem("a_done")
        v_full, v_done = sem("v_full"), sem("v_done")
        ssq_done = sem("ssq_done")
        rinv_done = sem("rinv_done")
        rstd_done = sem("rstd_done")
        h_done = sem("h_done")
        smax_done = sem("smax_done")
        exp_done = sem("exp_done")
        soft_done = sem("soft_done")
        merged_done = sem("merged_done")
        x_mixed = sem("x_mixed")
        top_shift = sem("top_shift")
        top_exp = sem("top_exp")
        expert_done = sem("expert_done")
        gelu_in = sem("gelu_in")
        tanh_done = sem("tanh_done")
        acc_step = sem("acc_step")
        dve_step = sem("dve_step")
        act_step = sem("act_step")
        slot_used = sem("slot_used")
        staged = sem("staged")
        stage_seen = sem("stage_seen")
        base_set = sem("base_set")
        out_in = sem("out_in")
        row_landed = [ctx.enter_context(nc.semaphore(f"row_landed{i}")) for i in range(RING)]
        GROUPS = HK // RING
        A_GATES = 1 + NT + NA // 2 + NA // 2 + NT * 2 * D // CW
        A_SCORES = A_GATES + HEADS + 2 * NT + NHP // 2
        A_ALL = A_SCORES + NT * NHP // 4
        PHASES = 2 * NT

        with nc.Block() as block:
            @block.sync
            def _(sp):
                sp.dma_start(xs[:, :, :], x[0].rearrange("(t p) d -> p t d", p=P)).then_inc(x_in, 16)
                sp.dma_start(cst[:, :], consts).then_inc(cst_in, 16)
                sp.wait_ge(x_in, 16)
                sp.wait_ge(cst_in, 16)

            @block.vector
            def _(dve):
                dve.memset(base[:, :], 0.0).then_inc(base_set, 1)
                dve.wait_ge(base_set, 1)

        for s in sems:
            nc.sync.sem_clear(s)
        nc.all_engine_barrier()

        with nc.Fori(0, depth) as layer:
            block_ctx = nc.Block()
            block = block_ctx.__enter__()

            @block.sync
            def _(sp):
                lay = bass.ds(layer, 1)

                def bcast(row):
                    return row.to_broadcast([P, D])

                def chunk(c):
                    if c < IN_CHUNKS:
                        w, n = w_in, c
                    elif c < IN_CHUNKS + OUT_CHUNKS:
                        w, n = w_out, c - IN_CHUNKS
                    else:
                        w, n = peer_wq, c - IN_CHUNKS - OUT_CHUNKS
                    if c >= W_SLOTS:
                        sp.wait_ge(w_used, c - W_SLOTS + 1)
                    sp.dma_start(wring[:, c % W_SLOTS, :, :],
                                 w[lay, :, n * CW:(n + 1) * CW].rearrange("l (k p) n -> p (l k) n", p=P)
                                 ).then_inc(w_landed[c % W_SLOTS], 16)

                sp.dma_start(gmix[:, :], bcast(mix_norm[lay, :])).then_inc(small_in, 16)
                for c in range(W_SLOTS):
                    chunk(c)
                sp.dma_start(gffn[:, :], bcast(ffn_norm[lay, :])).then_inc(small_in, 16)
                sp.dma_start(pscale[:, :], bcast(pool_scale[lay, :])).then_inc(small_in, 16)
                sp.dma_start(wpool[:, :, :], w_pool[lay, :, :, :].rearrange("l g c o -> c (l g) o")).then_inc(small_in, 16)
                sp.dma_start(keys[:, :, :], peer_keys[lay, :, :, :].rearrange("l a n d -> n (l a) d")).then_inc(small_in, 16)
                sp.dma_start(wup, w_attn_up[lay, :, :].rearrange("l (c p) n -> p (l c) n", p=P)).then_inc(small_in, 16)
                for c in range(W_SLOTS, IN_CHUNKS + OUT_CHUNKS + PQ_CHUNKS):
                    chunk(c)

            @block.gpsimd
            def _(pool):
                pool.wait_ge(a_done, A_ALL)
                for t in range(NT):
                    pool.wait_ge(expert_done, t + 1)
                    for side, rows in enumerate((u_rows, v_rows)):
                        phase = 2 * t + side
                        with pool.Fori(0, GROUPS) as i:
                            for half in range(2):
                                n = i * RING + half * HALF + phase * HK
                                pool.wait_ge(slot_used, n + HALF)
                                pool.tensor_copy(stage[:, half, :],
                                                 expert[:, t, bass.ds(i * RING + half * HALF, HALF)]
                                                 ).then_inc(staged, 1)
                                pool.wait_ge(staged, phase * 2 * GROUPS + 2 * i + half + 1)
                                pool.sem_inc(stage_seen, 1)
                                for r in range(HALF):
                                    slot = half * HALF + r
                                    pool.indirect_dma_start(
                                        ring[:, slot, :], None, rows,
                                        bass.IndirectOffsetOnAxis(ap=stage[:, half, r:r + 1], axis=0)
                                    ).then_inc(row_landed[slot], 16)

            @block.scalar
            def _(act):
                job = [0]

                def empty(dst, src_of, func=ACT.Copy, scale=1.0):
                    n = job[0]
                    job[0] += 1
                    act.wait_ge(a_full, n + 1)
                    act.activation(dst, src_of(abank[n % 4]), func, scale=scale).then_inc(a_done, 1)

                def norm(n):
                    for t in range(NT):
                        act.activation(h[:, t, :], xs[:, t, :], ACT.Square,
                                       accum_out=stat[:, 0, t:t + 1]).then_inc(ssq_done, 1)
                    act.wait_ge(rinv_done, n)
                    act.activation(stat[:, 2, :], stat[:, 1, :], ACT.Sqrt).then_inc(rstd_done, 1)

                def blocks(bank):
                    return bank[:, :].rearrange("p (k n) -> p k n", n=P)

                def pair(bank):
                    return bank[:, :].rearrange("p (k n) -> p k n", n=S)

                norm(1)
                act.wait_ge(small_in, 6 * 16)
                empty(keysT[:, :, :], lambda b: blocks(b)[:, 0:2, :])
                for t in range(NT):
                    empty(hT[:, 0:4, t * P:(t + 1) * P], blocks)
                for j in (0, 2):
                    empty(qT[:, j:j + 2, :], pair, scale=DH ** -0.5)
                for j in (0, 2):
                    empty(kT[:, j:j + 2, :], pair)
                for c in range(2 * D // CW):
                    for t in range(NT):
                        empty(gates[:, t, c * CW:(c + 1) * CW], lambda b: b[:, :], ACT.Sigmoid)
                for hd in range(HEADS):
                    act.wait_ge(smax_done, 2 * (hd + 1))
                    act.activation(soft[:, hd, 0:P], soft[:, hd, 0:P], ACT.Exp,
                                   bias=smax[:, hd, 0:1], accum_out=ssum[:, hd, 0:1]).then_inc(exp_done, 1)
                    act.activation(soft[:, hd, P:], soft[:, hd, P:], ACT.Exp,
                                   bias=smax[:, hd, 1:2], accum_out=ssum[:, hd, 1:2]).then_inc(exp_done, 1)
                for hd in range(HEADS):
                    empty(softT[:, hd, :], lambda b: b[:, 0:KEYS_ALL])
                for t in range(NT):
                    empty(hT[:, 0:4, t * P:(t + 1) * P], blocks)
                act.wait_ge(x_mixed, NT * 2)
                norm(2)
                for t in range(NT):
                    empty(hT[:, 0:4, t * P:(t + 1) * P], blocks)
                for a in range(0, NHP, 2):
                    empty(pqT[:, a:a + 2, :], pair)
                for t in range(NT):
                    for a in range(0, NHP, 4):
                        empty(score[:, t, a:a + 4, :], blocks)
                for t in range(NT):
                    act.wait_ge(top_shift, t + 1)
                    act.activation(prob[:, t, :], prob[:, t, :], ACT.Exp).then_inc(top_exp, 1)
                for t in range(NT):
                    act.wait_ge(gelu_in, t + 1)
                    act.activation(g2[:, :], g1[:, :], ACT.Tanh,
                                   scale=(2.0 / np.pi) ** 0.5).then_inc(tanh_done, 1)

            @block.tensor
            def _(pe):
                count = {"a": 0, "v": 0}
                banks = {"a": (abank, a_full, a_done), "v": (vbank, v_full, v_done)}

                def claim(kind):
                    bank, _, done = banks[kind]
                    n = count[kind]
                    if n >= 4:
                        pe.wait_ge(done, n - 3)
                    return bank[n % 4]

                def filled(kind, ins):
                    ins.then_inc(banks[kind][1], 1)
                    count[kind] += 1
                    return count[kind]

                def turn(src):
                    for half, kind in enumerate("av"):
                        b = claim(kind)
                        for j in range(4):
                            k = 4 * half + j
                            ins = pe.transpose(b[:, j * P:(j + 1) * P], src[:, k * P:(k + 1) * P], ident)
                        filled(kind, ins)

                def hT_ready():
                    pe.wait_ge(a_done, count["a"])
                    pe.wait_ge(v_done, count["v"])

                def weights(c):
                    pe.wait_ge(w_landed[c % W_SLOTS], 16 * (c // W_SLOTS + 1))
                    return wring[:, c % W_SLOTS]

                def rows_by(c, t, kind):
                    w, b = weights(c), claim(kind)
                    for k in range(KC):
                        ins = pe.matmul(b[:, :], hT[:, k, t * P:(t + 1) * P], w[:, k, :],
                                        start=(k == 0), stop=(k == KC - 1))
                    return filled(kind, ins)

                def cols_by(c, j, kind):
                    w, b = weights(c), claim(kind)
                    for m in range(2):
                        for k in range(KC):
                            ins = pe.matmul(b[:, m * S:(m + 1) * S], w[:, k, (j + m) * P:(j + m + 1) * P],
                                            hT[:, k, :], start=(k == 0), stop=(k == KC - 1))
                    return filled(kind, ins)

                def through(c):
                    pe.drain().then_inc(w_used, 1)

                pe.wait_ge(small_in, 6 * 16)
                b = claim("a")
                for a in range(2):
                    ins = pe.transpose(b[:, a * P:(a + 1) * P], keys[:, a, :], ident)
                filled("a", ins)
                for t in range(NT):
                    pe.wait_ge(h_done, t + 1)
                    turn(h[:, t, :])
                hT_ready()
                for t in range(NT):
                    p_done = rows_by(0, t, "v")
                through(0)
                for j in (0, 2):
                    cols_by(1, j, "a")
                through(1)
                for j in (0, 2):
                    k_done = cols_by(2, j, "a")
                through(2)
                for t in range(NT):
                    v_ready = rows_by(3, t, "v")
                through(3)

                pe.wait_ge(v_done, p_done)
                for g in range(0, NG, 2):
                    b = claim("v")
                    for m in range(2):
                        for s in range(NT):
                            ins = pe.matmul(b[:, m * S:(m + 1) * S], p_sb[:, s, (g + m) * P:(g + m + 1) * P],
                                            band[:, g + m, s, :], start=(s == 0), stop=(s == NT - 1))
                    m_done = filled("v", ins)

                pe.wait_ge(a_done, k_done)
                for hd in range(HEADS):
                    o, c = (hd % 2) * DH, hd // 2
                    b = claim("v")
                    pe.matmul(b[:, 0:P], qT[o:o + DH, c, 0:P], kT[o:o + DH, c, 0:P], start=True, stop=True)
                    ins = pe.matmul(b[:, P:KEYS_ALL], qT[o:o + DH, c, P:S], kT[o:o + DH, c, :],
                                    start=True, stop=True)
                    filled("v", ins)
                    rows_by(4 + hd // 2, hd % 2, "a")
                    if hd % 2 == 1:
                        through(4 + hd // 2)

                for t in range(NT):
                    for g in range(0, NG, 2):
                        b = claim("v")
                        for m in range(2):
                            ins = pe.matmul(b[:, m * GOUT:(m + 1) * GOUT], mT[:, g + m, t * P:(t + 1) * P],
                                            wpool[:, g + m, :], start=True, stop=True)
                        filled("v", ins)

                for hd in range(HEADS):
                    pe.wait_ge(soft_done, 2 * (hd + 1))
                    b = claim("a")
                    for m in range(3):
                        ins = pe.transpose(b[:, m * P:(m + 1) * P], soft[:, hd, m * P:(m + 1) * P], ident)
                    softT_done = filled("a", ins)
                    if hd % 2 == 1:
                        pe.wait_ge(a_done, softT_done)
                        b = claim("v")
                        for e in (hd - 1, hd):
                            o = (e % 2) * DH
                            val = [v_sb[:, s, e * DH:(e + 1) * DH] for s in range(NT)]
                            pe.matmul(b[o:o + DH, 0:P], val[0], softT[:, e, 0:P], start=True, stop=True)
                            pe.matmul(b[o:o + DH, P:S], val[0], softT[:, e, P:2 * P], start=True, stop=False)
                            ins = pe.matmul(b[o:o + DH, P:S], val[1], softT[:, e, 2 * P:], start=False, stop=True)
                        o_done = filled("v", ins)
                pe.wait_ge(v_done, o_done)
                for t in range(NT):
                    for n in range(2):
                        b = claim("v")
                        for c in range(NA):
                            ins = pe.matmul(b[:, :], oT[:, c, t * P:(t + 1) * P], wup[:, c, n * CW:(n + 1) * CW],
                                            start=(c == 0), stop=(c == NA - 1))
                        filled("v", ins)
                for t in range(NT):
                    pe.wait_ge(merged_done, 2 * (t + 1))
                    turn(h[:, t, :])
                hT_ready()
                for c in range(OUT_CHUNKS):
                    for t in range(NT):
                        rows_by(IN_CHUNKS + c, t, "v")
                    through(IN_CHUNKS + c)

                for t in range(NT):
                    pe.wait_ge(h_done, NT + t + 1)
                    turn(h[:, t, :])
                hT_ready()
                for c in range(PQ_CHUNKS):
                    for j in (0, 2):
                        pq_done = cols_by(IN_CHUNKS + OUT_CHUNKS + c, j, "a")
                    through(IN_CHUNKS + OUT_CHUNKS + c)
                pe.wait_ge(a_done, pq_done)
                for t in range(NT):
                    for a in range(0, NHP, 4):
                        b = claim("a")
                        for m in range(4):
                            ins = pe.matmul(b[:, m * NK:(m + 1) * NK], pqT[:, a + m, t * P:(t + 1) * P],
                                            keysT[:, (a + m) % 2, :], start=True, stop=True)
                        filled("a", ins)

            @block.vector
            def _(dve):
                job = [0]
                steps = [0]

                def bank():
                    dve.wait_ge(v_full, job[0] + 1)
                    return vbank[job[0] % 4]

                def emptied(ins):
                    ins.then_inc(v_done, 1)
                    job[0] += 1

                def step(ins):
                    ins.then_inc(dve_step, 1)
                    steps[0] += 1

                def settle():
                    dve.wait_ge(dve_step, steps[0])

                def blocks(b):
                    return b[:, :].rearrange("p (k n) -> p k n", n=P)

                def norm(n, gain):
                    dve.wait_ge(ssq_done, NT * n)
                    step(dve.tensor_scalar(stat[:, 1, :], stat[:, 0, :], 1.0 / D, EPS, ALU.mult, ALU.add))
                    settle()
                    dve.reciprocal(stat[:, 1, :], stat[:, 1, :]).then_inc(rinv_done, 1)
                    dve.wait_ge(rstd_done, n)
                    for t in range(NT):
                        dve.scalar_tensor_tensor(out=h[:, t, :], in0=xs[:, t, :], scalar=stat[:, 2, t:t + 1],
                                                 in1=gain[:, :], op0=ALU.mult, op1=ALU.mult).then_inc(h_done, 1)

                def turned():
                    for t in range(NT):
                        emptied(dve.tensor_copy(hT[:, 4:8, t * P:(t + 1) * P], blocks(bank())))

                dve.memset(tmp[:, 0, 0:2], 0.0).then_inc(slot_used, RING)
                dve.wait_ge(slot_used, RING)
                dve.wait_ge(small_in, 6 * 16)
                norm(1, gmix)
                turned()
                for t in range(NT):
                    emptied(dve.tensor_copy(p_sb[:, t, :], bank()[:, :]))
                for t in range(NT):
                    emptied(dve.tensor_copy(v_sb[:, t, :], bank()[:, :]))
                for g in range(0, NG, 2):
                    emptied(dve.tensor_copy(mT[:, g:g + 2, :], bank()[:, :].rearrange("p (k n) -> p k n", n=S)))

                for hd in range(HEADS):
                    slope = 2.0 ** (-8.0 * (hd + 1) / HEADS)
                    emptied(dve.scalar_tensor_tensor(out=soft[:, hd, :], in0=dist, scalar=slope,
                                                     in1=bank()[:, 0:KEYS_ALL], op0=ALU.mult, op1=ALU.add))
                    dve.wait_ge(v_done, job[0])
                    for t, (lo, hi) in enumerate(((0, P), (P, KEYS_ALL))):
                        dve.tensor_reduce(smax[:, hd, t:t + 1], soft[:, hd, lo:hi], AX.X, ALU.max,
                                          negate=True).then_inc(smax_done, 1)

                def gate(t, side, n):
                    lo = side * D + n * CW
                    return gates[:, t, lo:lo + CW]

                for t in range(NT):
                    for n in range(2):
                        cols = slice(n * CW, (n + 1) * CW)
                        emptied(dve.tensor_tensor(h[:, t, cols], bank()[:, :], pscale[:, cols], ALU.mult))
                        dve.wait_ge(v_done, job[0])
                        dve.wait_ge(a_done, A_GATES)
                        step(dve.tensor_tensor(h[:, t, cols], h[:, t, cols], gate(t, 0, n), ALU.mult))

                for hd in range(HEADS):
                    dve.wait_ge(exp_done, 2 * (hd + 1))
                    step(dve.reciprocal(srec[:, hd, :], ssum[:, hd, :]))
                    settle()
                    for t, (lo, hi) in enumerate(((0, P), (P, KEYS_ALL))):
                        dve.tensor_scalar(soft[:, hd, lo:hi], soft[:, hd, lo:hi], srec[:, hd, t:t + 1], None,
                                          ALU.mult).then_inc(soft_done, 1)
                for c in range(NA):
                    emptied(dve.tensor_copy(oT[:, c, :], bank()[:, 0:S]))

                for t in range(NT):
                    for n in range(2):
                        cols = slice(n * CW, (n + 1) * CW)
                        if 2 * t + n >= 2:
                            dve.wait_ge(merged_done, 2 * t + n - 1)
                        emptied(dve.tensor_tensor(tmp[:, n, :], bank()[:, :], gate(t, 1, n), ALU.mult))
                        dve.wait_ge(v_done, job[0])
                        dve.tensor_tensor(h[:, t, cols], h[:, t, cols], tmp[:, n, :],
                                          ALU.add).then_inc(merged_done, 1)
                turned()
                for c in range(OUT_CHUNKS):
                    cols = slice(c * CW, (c + 1) * CW)
                    for t in range(NT):
                        job[0] += 1
                        dve.wait_ge(v_full, job[0])
                        dve.tensor_tensor(xs[:, t, cols], xs[:, t, cols], vbank[(job[0] - 1) % 4][:, :],
                                          ALU.add).then_inc(x_mixed, 1)
                        dve.wait_ge(x_mixed, c * NT + t + 1)
                        dve.engine_nop().then_inc(v_done, 1)
                norm(2, gffn)
                turned()

                def search(vals, idxs, data, n):
                    for r in range(n):
                        step(dve.max(vals(r)[:, 0:8], data(r)))
                    settle()
                    for r in range(n):
                        step(dve.max_index(idxs(r)[:, 0:8], vals(r)[:, 0:8], data(r)))
                    settle()
                    for r in range(n):
                        step(dve.match_replace(data(r), vals(r)[:, 0:8], data(r), LOWEST))
                    settle()
                    for r in range(n):
                        step(dve.max(vals(r)[:, 8:16], data(r)))
                    settle()
                    for r in range(n):
                        step(dve.max_index(idxs(r)[:, 8:16], vals(r)[:, 8:16], data(r)))
                    settle()

                def choose(t):
                    dve.wait_ge(a_done, A_SCORES + (t + 1) * NHP // 4)
                    search(lambda r: sv[:, r, :], lambda r: si[:, r, :], lambda r: score[:, t, r, :], NHP)
                    halves = sv[:, :, :].rearrange("p (h a) i -> p h a i", a=2)
                    sums = cand[:, :, :].rearrange("p h (i j) -> p h i j", i=TOPK)
                    first = halves[:, :, 0, :].unsqueeze(3).to_broadcast([P, PH, TOPK, TOPK])
                    second = halves[:, :, 1, :].unsqueeze(2).to_broadcast([P, PH, TOPK, TOPK])
                    step(dve.tensor_tensor(sums, first, second, ALU.add))
                    step(dve.tensor_copy(sif[:, :, :], si[:, :, :]))
                    settle()
                    search(lambda r: cv[:, r, :], lambda r: ci[:, r * TOPK:(r + 1) * TOPK],
                           lambda r: cand[:, r, :], PH)
                    p3 = prob[:, t, :].rearrange("p (h k) -> p h k", h=PH)
                    dve.tensor_tensor(p3, cv[:, :, :], cv[:, :, 0:1].to_broadcast([P, PH, TOPK]),
                                      ALU.subtract).then_inc(top_shift, 1)
                    step(dve.tensor_scalar(cab[:, 0, :], ci[:, :], 4, None, ALU.logical_shift_right))
                    step(dve.tensor_scalar(cab[:, 1, :], ci[:, :], TOPK - 1, None, ALU.bitwise_and))
                    settle()
                    step(dve.tensor_copy(cabf[:, :, :], cab[:, :, :]))
                    settle()
                    hot = cand[:, :, :].rearrange("p h (k i) -> p (h k) i", i=TOPK)
                    hot4 = cand[:, :, :].rearrange("p h (k i) -> p h k i", i=TOPK)
                    ids = sif[:, :, :].rearrange("p (h a) i -> p h a i", a=2)
                    for a in range(2):
                        step(dve.tensor_tensor(hot, cabf[:, a, :].unsqueeze(2).to_broadcast([P, HK, TOPK]),
                                               iota16.unsqueeze(1).to_broadcast([P, HK, TOPK]), ALU.is_equal))
                        settle()
                        step(dve.tensor_tensor(hot4, hot4,
                                               ids[:, :, a, :].unsqueeze(2).to_broadcast([P, PH, TOPK, TOPK]),
                                               ALU.mult))
                        settle()
                        step(dve.tensor_reduce(picked[:, a, :], hot, AX.X, ALU.add))
                        settle()
                    step(dve.scalar_tensor_tensor(out=picked[:, 0, :], in0=picked[:, 0, :], scalar=float(NK),
                                                  in1=picked[:, 1, :], op0=ALU.mult, op1=ALU.add))
                    settle()
                    dve.tensor_scalar(expert[:, t, :], picked[:, 0, :], base[:, 0:1], None,
                                      ALU.add).then_inc(expert_done, 1)
                    dve.wait_ge(top_exp, t + 1)
                    step(dve.tensor_reduce(gsum[:, :], p3, AX.X, ALU.add))
                    settle()
                    step(dve.reciprocal(gsum[:, :], gsum[:, :]))
                    settle()
                    step(dve.tensor_tensor(p3, p3, gsum[:, :].unsqueeze(2).to_broadcast([P, PH, TOPK]),
                                           ALU.mult))
                    settle()

                def landed(phase, i, slot):
                    dve.wait_ge(row_landed[slot], layer * (16 * PHASES * GROUPS) + i * 16
                                + (16 * (phase * GROUPS + 1)))

                def u_pass(t):
                    with dve.Fori(0, GROUPS) as i:
                        for slot in range(RING):
                            landed(2 * t, i, slot)
                            dve.scalar_tensor_tensor(
                                out=ring[:, slot, :], in0=ring[:, slot, :], scalar=1.0, in1=h[:, t, :],
                                op0=ALU.mult, op1=ALU.mult,
                                accum_out=dots[:, bass.ds(i * RING + slot, 1)]).then_inc(slot_used, 1)

                def weigh(t):
                    dve.wait_ge(slot_used, RING + (2 * t + 1) * HK)
                    step(dve.tensor_tensor(g1[:, :], dots[:, :], dots[:, :], ALU.mult))
                    settle()
                    step(dve.tensor_scalar(g1[:, :], g1[:, :], 0.044715, 1.0, ALU.mult, ALU.add))
                    settle()
                    dve.tensor_tensor(g1[:, :], g1[:, :], dots[:, :], ALU.mult).then_inc(gelu_in, 1)
                    step(dve.scalar_tensor_tensor(out=wgt[:, :], in0=dots[:, :], scalar=0.5, in1=prob[:, t, :],
                                                  op0=ALU.mult, op1=ALU.mult))
                    step(dve.memset(acc[:, 0, :], 0.0))
                    settle()
                    dve.wait_ge(tanh_done, t + 1)
                    step(dve.scalar_tensor_tensor(out=wgt[:, :], in0=g2[:, :], scalar=1.0, in1=wgt[:, :],
                                                  op0=ALU.add, op1=ALU.mult))
                    settle()

                def v_pass(t):
                    step0 = 1 + t * HK
                    with dve.Fori(0, GROUPS) as i:
                        for slot in range(RING):
                            landed(2 * t + 1, i, slot)
                            dve.wait_ge(acc_step, i * RING + (step0 + slot))
                            dve.scalar_tensor_tensor(
                                out=acc[:, (slot + 1) % 2, :], in0=ring[:, slot, :],
                                scalar=wgt[:, bass.ds(i * RING + slot, 1)], in1=acc[:, slot % 2, :],
                                op0=ALU.mult, op1=ALU.add).then_inc(acc_step, 1)
                            dve.engine_nop().then_inc(slot_used, 1)
                    dve.wait_ge(acc_step, step0 + HK)
                    step(dve.tensor_tensor(xs[:, t, :], xs[:, t, :], acc[:, 0, :], ALU.add))
                    settle()

                for t in range(NT):
                    choose(t)
                dve.sem_inc(acc_step, 1)
                for t in range(NT):
                    u_pass(t)
                    weigh(t)
                    v_pass(t)
                step(dve.tensor_scalar(base[:, :], base[:, :], float(EXPERTS), None, ALU.add))
                settle()

            block_ctx.__exit__(None, None, None)
            for s in sems:
                nc.sync.sem_clear(s)
            nc.all_engine_barrier()

        with nc.Block() as block:
            @block.sync
            def _(sp):
                sp.dma_start(gmix[:, :], final_norm.unsqueeze(0).to_broadcast([P, D])).then_inc(small_in, 16)
                for t in range(NT):
                    sp.wait_ge(h_done, t + 1)
                    sp.dma_start(out[0, t * P:(t + 1) * P, :], h[:, t, :]).then_inc(out_in, 16)
                sp.wait_ge(out_in, 16 * NT)

            @block.scalar
            def _(act):
                for t in range(NT):
                    act.activation(h[:, t, :], xs[:, t, :], ACT.Square,
                                   accum_out=stat[:, 0, t:t + 1]).then_inc(ssq_done, 1)
                act.wait_ge(rinv_done, 1)
                act.activation(stat[:, 2, :], stat[:, 1, :], ACT.Sqrt).then_inc(rstd_done, 1)

            @block.vector
            def _(dve):
                dve.wait_ge(ssq_done, NT)
                dve.tensor_scalar(stat[:, 1, :], stat[:, 0, :], 1.0 / D, EPS, ALU.mult,
                                  ALU.add).then_inc(dve_step, 1)
                dve.wait_ge(dve_step, 1)
                dve.reciprocal(stat[:, 1, :], stat[:, 1, :]).then_inc(rinv_done, 1)
                dve.wait_ge(small_in, 16)
                dve.wait_ge(rstd_done, 1)
                for t in range(NT):
                    dve.scalar_tensor_tensor(out=h[:, t, :], in0=xs[:, t, :], scalar=stat[:, 2, t:t + 1],
                                             in1=gmix[:, :], op0=ALU.mult, op1=ALU.mult).then_inc(h_done, 1)


_INS = ["x", "mix_norm", "w_in", "w_pool", "pool_scale", "w_attn_up", "w_out", "ffn_norm", "peer_wq",
        "peer_keys", "peer_u", "peer_v", "final_norm"]


def kernel(**inputs):
    import concourse.bacc as bacc
    from concourse.bass_utils import run_bass_kernel_spmd

    nc = bacc.Bacc("TRN2", target_bir_lowering=False, num_devices=1)
    arrays, args = {}, []
    for name, a in [("consts", constants())] + [(n, inputs[n]) for n in _INS]:
        a = np.ascontiguousarray(a)
        arrays[f"in_{name}"] = a
        args.append(nc.dram_tensor(f"in_{name}", a.shape, mybir.dt.from_np(a.dtype), kind="ExternalInput").ap())
    out = nc.dram_tensor("trunk_out", (1, S, D), F32, kind="ExternalOutput").ap()
    build(nc, *args, out)
    r = run_bass_kernel_spmd(nc, [arrays], core_ids=[0])
    return r.results[0]["trunk_out"]
```

```python
from contextlib import ExitStack

import numpy as np
import concourse.bass as bass
from concourse import mybir

F32 = mybir.dt.float32
U32 = mybir.dt.uint32
ALU = mybir.AluOpType
ACT = mybir.ActivationFunctionType
AX = mybir.AxisListType

P = 128
S = 256
NT = S // P
D = 1024
KC = D // P
HEADS, DH = 8, 64
WINDOWS = (2, 4, 8, 16)
NG = len(WINDOWS)
GOUT = D // NG
AW = HEADS * DH
NA = AW // P
PH, NK, TOPK = 8, 128, 16
NHP = 2 * PH
HK = PH * TOPK
EXPERTS = NK * NK
EPS = 1e-6
LOWEST = -3.0e38
MASKED = -1.0e30
BANK = 512

CW = 256
UPW = 512
IN_CHUNKS = (4 * AW + 2 * D) // CW
UP_CHUNKS = D // UPW
OUT_CHUNKS = D // CW
PQ_CHUNKS = PH * 2 * P // CW
C_P, C_Q, C_K, C_V = (i * AW // CW for i in range(4))
C_GATE = 4 * AW // CW
C_UP = IN_CHUNKS
C_OUT = C_UP + UP_CHUNKS
C_PQ = C_OUT + OUT_CHUNKS
CHUNKS = C_PQ + PQ_CHUNKS
W_SLOTS = 4

HEAD_PAIRS = [(hd, hd + 2) for hd in range(HEADS) if hd % 4 < 2]

RING = 16
HALF = RING // 2
TRIPS = HK // RING
PE_SLOTS = (1, 4, 7, 9, 12, 15)
DVE_SLOTS = tuple(r for r in range(RING) if r not in PE_SLOTS)
PE_HALF, DVE_HALF = len(PE_SLOTS) // 2, len(DVE_SLOTS) // 2
DIAGS = 3
V_BRANCHES = 8

A_HEAD = 1 + 2
A_P, A_Q, A_K, A_V = (A_HEAD + i for i in range(1, 5))
A_WIDE = A_V + 2 * D // BANK
A_POOL = A_WIDE + 1
A_GATE_A = A_POOL + D // BANK
A_SOFT = A_GATE_A + HEADS // 2
A_GATE_B1 = A_SOFT + 1
A_O = A_GATE_B1 + 1
A_GATE_B = A_O + 1
A_MERGED = A_GATE_B + 2
A_H2 = A_MERGED + 2
A_PQ = [A_H2 + n for n in (1, 2, 4, 6)]
A_SCORE = [A_H2 + n for n in (3, 5, 7, 8)]
A_ALL = A_SCORE[-1]

C_ID = 0
C_IOTA = C_ID + P
C_DIST = C_IOTA + TOPK
C_BAND = C_DIST + NT * S
C_BASE = C_BAND + NT * NG * NT * P


def constants(depth):
    c = np.zeros((P, C_BASE + depth * NT), np.float32)
    c[:, C_ID:C_ID + P] = np.eye(P, dtype=np.float32)
    c[:, C_IOTA:C_IOTA + TOPK] = np.arange(TOPK)
    dist = c[:, C_DIST:C_BAND].reshape(P, NT, S)
    band = c[:, C_BAND:C_BASE].reshape(P, NT, NG, NT, P)
    for tile in range(NT):
        q, k = np.arange(P)[:, None] + tile * P, np.arange(S)[None, :]
        dist[:, tile] = np.where(k <= q, k - q, MASKED)
        t, src = np.arange(P) + tile * P, np.arange(S)[:, None]
        for g, w in enumerate(WINDOWS):
            inside = (src <= t) & (src > t - w)
            m = np.where(inside, 1.0 / np.minimum(t + 1, w), 0.0) - (src == t)
            band[:, tile, g] = m.reshape(NT, P, P).transpose(1, 0, 2)
    c[:, C_BASE:] = np.repeat(np.arange(depth), NT) * EXPERTS
    return c


def build(nc, consts, x, mix_norm, w_in, w_pool, pool_scale, w_attn_up, w_out, ffn_norm, peer_wq,
          peer_keys, peer_u, peer_v, final_norm, out):
    depth = mix_norm.shape[0]
    windows = depth * NT
    table_rows = (peer_u.rearrange("l n d -> (l n) d"), peer_v.rearrange("l n d -> (l n) d"))

    with ExitStack() as ctx:
        def sb(name, shape, dt=F32):
            return ctx.enter_context(nc.sbuf_tensor(name, shape, dt))

        sems = []

        def sem(name):
            s = ctx.enter_context(nc.semaphore(name))
            sems.append(s)
            return s

        cst = sb("cst", [P, C_BASE + windows])
        ident = cst[:, C_ID:C_ID + P]
        iota16 = cst[:, C_IOTA:C_IOTA + TOPK]

        xs = sb("xs", [P, NT * D])
        hn = sb("hn", [P, D])
        hT = sb("hT", [P, KC, P])
        gains = sb("gains", [2 * KC, P])
        gainT = sb("gainT", [P, 2, KC])
        ones = sb("ones", [1, P])
        wide = sb("wide", [P, 2 * D])
        gffn, pscale = wide[:, 0:D], wide[:, D:2 * D]
        wpool = sb("wpool", [P, NG, GOUT])
        keys = sb("keys", [P, 2, P])
        keysT = sb("keysT", [P, 2, NK])
        wring = sb("wring", [P, W_SLOTS, KC * CW])
        p_sb = sb("p_sb", [P, NT * AW])
        v_sb = sb("v_sb", [P, NT * AW])
        kT = sb("kT", [P, NA, S])
        qT = sb("qT", [P, NA, P])
        mT = sb("mT", [P, NG, P])
        oT = sb("oT", [P, NA, P])
        stat = sb("stat", [P, 3])
        smax = sb("smax", [P, HEADS])
        ssum = sb("ssum", [P, HEADS])
        srec = sb("srec", [P, HEADS])
        sv = sb("sv", [P, NHP, TOPK])
        si = sb("si", [P, NHP, TOPK], U32)
        sif = sb("sif", [P, NHP, TOPK])
        cv = sb("cv", [P, PH, TOPK])
        ci = sb("ci", [P, HK], U32)
        cab = sb("cab", [P, 2, HK], U32)
        cabf = sb("cabf", [P, 2, HK])
        picked = sb("picked", [P, 2, HK])
        gsum = sb("gsum", [P, PH])
        base = sb("base", [P, 1])
        prob = sb("prob", [P, HK])
        expert = sb("expert", [P, HK], U32)

        buf1 = sb("buf1", [P, 2 * D])
        gates = buf1[:, :]
        pqT = buf1[:, :].rearrange("p (a n) -> p a n", a=NHP)
        buf2 = sb("buf2", [P, HEADS * S])
        soft = buf2[:, :].rearrange("p (h n) -> p h n", h=HEADS)
        score = buf2[:, :].rearrange("p (a k) -> p a k", a=NHP)
        buf3 = sb("buf3", [P, HEADS * S])
        softT = buf3[:, :].rearrange("p (h n) -> p h n", h=HEADS)
        rows = buf3[0:1, :]
        tmp = buf3[:, 0:D]
        cand = buf3[:, :].rearrange("p (h n) -> p h n", h=PH)

        ring = sb("ring", [P, RING, D])
        tok = sb("tok", [P, D])
        prob_g = sb("prob_g", [P, HK])
        expert_g = sb("expert_g", [P, HK], U32)
        stage = sb("stage", [P, 2, HALF], U32)
        acc = sb("acc", [P, D])
        diag = sb("diag", [P, DIAGS, P])
        dots = sb("dots", [P, HK])
        g1 = sb("g1", [P, HK])
        g2 = sb("g2", [P, HK])
        wgt = sb("wgt", [P, HK])

        abank = [ctx.enter_context(nc.psum_tensor(f"abank{i}", [P, BANK], F32)) for i in range(4)]
        vbank = [ctx.enter_context(nc.psum_tensor(f"vbank{i}", [P, BANK], F32)) for i in range(4)]

        row_landed = [ctx.enter_context(nc.semaphore(f"row_landed{i}")) for i in range(RING)]
        start_in = sem("start_in")
        tables_in = sem("tables_in")
        x_in = sem("x_in")
        x_rest_in = sem("x_rest_in")
        cleared = sem("cleared")
        first_in = sem("first_in")
        first_w_in = [sem(f"first_w_in{i}") for i in range(W_SLOTS)]
        head_in = sem("head_in")
        small_in = sem("small_in")
        FIRST, SMALL = 3 * 16, 3 * 16
        w_landed = [sem(f"w_landed{i}") for i in range(W_SLOTS)]
        w_used = sem("w_used")
        a_full, a_done = sem("a_full"), sem("a_done")
        v_full, v_done = sem("v_full"), sem("v_done")
        ssq_done = sem("ssq_done")
        rinv_done = sem("rinv_done")
        root_done = sem("root_done")
        hn_done = sem("hn_done")
        gain_done = sem("gain_done")
        smax_done = sem("smax_done")
        exp_done = sem("exp_done")
        srec_done = sem("srec_done")
        soft_done = sem("soft_done")
        merged_done = sem("merged_done")
        x_mixed = sem("x_mixed")
        top_shift = sem("top_shift")
        top_exp = sem("top_exp")
        handed = sem("handed")
        expert_ready = sem("expert_ready")
        expert_taken = sem("expert_taken")
        gelu_in = sem("gelu_in")
        tanh_done = sem("tanh_done")
        dve_step = sem("dve_step")
        u_step = sem("u_step")
        v_step = sem("v_step")
        wgt_done = sem("wgt_done")
        diag_done = sem("diag_done")
        v_summed = sem("v_summed")
        staged = sem("staged")
        stage_seen = sem("stage_seen")
        x_final = sem("x_final")
        out_in = sem("out_in")

        def x_of(tile):
            return xs[:, bass.ds(tile * D, D)]

        def blocks(b):
            return b[:, :].rearrange("p (k n) -> p k n", n=P)


        def chunk(sp, lay, c, signal):
            slot = wring[:, c % W_SLOTS, :]
            if C_UP <= c < C_OUT:
                w, n, width = w_attn_up, c - C_UP, UPW
            else:
                w, n = ((w_in, c) if c < C_UP else
                        (w_out, c - C_OUT) if c < C_PQ else (peer_wq, c - C_PQ))
                width = CW
            sp.dma_start(slot.rearrange("p (k n) -> p k n", n=width),
                         w[bass.ds(lay, 1), :, n * width:(n + 1) * width].rearrange("l (k p) n -> p (l k) n", p=P)
                         ).then_inc(signal, 16)

        def gains_and_keys(sp, lay, signal):
            one = bass.ds(lay, 1)
            for n, g in enumerate((mix_norm, ffn_norm)):
                sp.dma_start(gains[n * KC:(n + 1) * KC, :], g[one, :].rearrange("l (k p) -> (l k) p", p=P)).then_inc(signal, 16)
            sp.dma_start(keys[:, :, :], peer_keys[one, :, :, :].rearrange("l a n d -> n (l a) d")).then_inc(signal, 16)

        def sync_head(sp, lay):
            gains_and_keys(sp, lay, head_in)
            for c in range(CHUNKS - W_SLOTS, CHUNKS):
                sp.wait_ge(w_used, c + 1)
                chunk(sp, lay, c % W_SLOTS, head_in)
            sp.wait_ge(head_in, FIRST + W_SLOTS * 16)

        def mix_sync(sp, lay):
            one = bass.ds(lay, 1)
            for n, g in enumerate((ffn_norm, pool_scale)):
                sp.dma_start(rows[:, n * D:(n + 1) * D], g[one, :]).then_inc(small_in, 16)
            sp.dma_start(wpool[:, :, :], w_pool[one, :, :, :].rearrange("l g c o -> c (l g) o")).then_inc(small_in, 16)
            for c in range(W_SLOTS, CHUNKS):
                sp.wait_ge(w_used, c - W_SLOTS + 1)
                chunk(sp, lay, c, w_landed[c % W_SLOTS])

        def mix_scalar(act, tile, copied, early, late, width=S):
            job = [0]

            def bank():
                act.wait_ge(a_full, job[0] + 1)
                return abank[job[0] % 4]

            def emptied(ins):
                ins.then_inc(a_done, 1)
                job[0] += 1

            def copy_out(dst, view=blocks, func=ACT.Copy, scale=1.0):
                emptied(act.activation(dst, view(bank()), func, scale=scale))

            def norm(n, junk):
                act.activation(junk, x_of(tile), ACT.Square, accum_out=stat[:, 0:1]).then_inc(ssq_done, 1)
                act.wait_ge(rinv_done, n + 1)
                act.activation(stat[:, 2:3], stat[:, 1:2], ACT.Sqrt).then_inc(root_done, 1)
                act.wait_ge(root_done, n + 1)
                act.activation(hn[:, :], x_of(tile), ACT.Copy, scale=stat[:, 2:3]).then_inc(hn_done, 1)

            def turned(n):
                for half in range(2):
                    b = bank()
                    for j in range(4):
                        k = 4 * half + j
                        ins = act.activation(hT[:, k, :], b[:, j * P:(j + 1) * P], ACT.Copy,
                                             scale=gainT[:, n, k:k + 1])
                    emptied(ins)

            copied()
            norm(0, gates[:, 0:D])
            b = bank()
            act.activation(keysT[:, :, :], blocks(b)[:, 0:2, :], ACT.Copy)
            emptied(act.activation(gainT[:, :, :], b[:, 2 * P:2 * P + 2 * KC].rearrange("p (n k) -> p n k", n=2),
                                   ACT.Copy))
            act.wait_ge(a_done, 1)
            turned(0)
            copy_out(p_sb[:, bass.ds(tile * AW, AW)], lambda b: b[:, :])
            copy_out(qT[:, :, :], scale=DH ** -0.5)
            copy_out(kT[:, :, bass.ds(tile * P, P)])
            copy_out(v_sb[:, bass.ds(tile * AW, AW)], lambda b: b[:, :])
            for c in range(2 * D // BANK):
                copy_out(wide[:, c * BANK:(c + 1) * BANK], lambda b: b[:, :])
            copy_out(mT[:, :, :])
            for n, hd in enumerate(hd for heads in HEAD_PAIRS for hd in heads):
                act.wait_ge(smax_done, n + 1)
                act.activation(soft[:, hd, 0:width], soft[:, hd, 0:width], ACT.Exp, bias=smax[:, hd:hd + 1],
                               accum_out=ssum[:, hd:hd + 1]).then_inc(exp_done, 1)
            act.wait_ge(srec_done, 1)
            for hd in range(HEADS):
                act.activation(soft[:, hd, 0:width], soft[:, hd, 0:width], ACT.Copy,
                               scale=srec[:, hd:hd + 1]).then_inc(soft_done, 1)

            def gate(c):
                copy_out(gates[:, c * BANK:(c + 1) * BANK], lambda b: b[:, :], ACT.Sigmoid)

            gate(0)
            gate(1)
            for hd in range(0, HEADS, 2):
                copy_out(softT[:, hd:hd + 2, 0:width],
                         lambda b: b[:, :].rearrange("p (h n) -> p h n", n=S)[:, :, 0:width])
            gate(2)
            copy_out(oT[:, :, :])
            gate(3)
            for half in range(2):
                copy_out(hT[:, 4 * half:4 * half + 4, :])
            act.wait_ge(x_mixed, 2)
            act.wait_ge(merged_done, 2)
            norm(1, gates[:, 0:D])
            turned(1)
            for n in range(5):
                if n < 4:
                    copy_out(pqT[:, 4 * n:4 * n + 4, :])
                if n >= 1:
                    copy_out(score[:, 4 * n - 4:4 * n, :])
            early()
            act.wait_ge(top_shift, 1)
            act.activation(prob[:, :], prob[:, :], ACT.Exp).then_inc(top_exp, 1)
            late()

        def mix_tensor(pe, tile, alone=False):
            sources = 1 if alone else NT
            count = {"a": 0, "v": 0}
            banks = {"a": (abank, a_full, a_done), "v": (vbank, v_full, v_done)}

            def claim(kind):
                bank, _, done = banks[kind]
                n = count[kind]
                if n >= 4:
                    pe.wait_ge(done, n - 3)
                return bank[n % 4]

            def filled(kind, ins):
                ins.then_inc(banks[kind][1], 1)
                count[kind] += 1

            def turn(src, n):
                for k in range(0, n, 4):
                    b = claim("a")
                    for j in range(min(4, n - k)):
                        ins = pe.transpose(b[:, j * P:(j + 1) * P], src(k + j), ident)
                    filled("a", ins)

            def weights(c, width=CW):
                if c >= W_SLOTS:
                    pe.wait_ge(w_landed[c % W_SLOTS], 16 * (c // W_SLOTS))
                elif alone:
                    pe.wait_ge(first_w_in[c], 16)
                return wring[:, c % W_SLOTS, :].rearrange("p (k n) -> p k n", n=width)

            def through(c):
                pe.drain().then_inc(w_used, 1)

            def rows_by(c, kind):
                b = claim(kind)
                for m in range(BANK // CW):
                    w = weights(c + m)
                    for k in range(KC):
                        ins = pe.matmul(b[:, m * CW:(m + 1) * CW], hT[:, k, :], w[:, k, :],
                                        start=(k == 0), stop=(k == KC - 1))
                    if m == BANK // CW - 1:
                        filled(kind, ins)
                    through(c + m)

            def cols_by(c):
                b = claim("a")
                for m in range(BANK // P):
                    cc, lo = c + m * P // CW, m * P % CW
                    w = weights(cc)
                    for k in range(KC):
                        ins = pe.matmul(b[:, m * P:(m + 1) * P], w[:, k, lo:lo + P], hT[:, k, :],
                                        start=(k == 0), stop=(k == KC - 1))
                    if m == BANK // P - 1:
                        filled("a", ins)
                    if lo + P == CW:
                        through(cc)

            if alone:
                pe.wait_ge(first_in, FIRST)
            b = claim("a")
            for a in range(2):
                pe.transpose(b[:, a * P:(a + 1) * P], keys[:, a, :], ident)
            filled("a", pe.transpose(b[:, 2 * P:2 * P + 2 * KC], gains[:, :], ident[0:2 * KC, 0:2 * KC]))
            pe.wait_ge(hn_done, 1)
            turn(lambda k: hn[:, k * P:(k + 1) * P], KC)
            pe.wait_ge(a_done, A_HEAD)
            rows_by(C_P, "a")
            cols_by(C_Q)
            cols_by(C_K)
            rows_by(C_V, "a")

            pe.wait_ge(small_in, SMALL)
            for c in range(2 * D // BANK):
                filled("a", pe.matmul(claim("a")[:, :], ones[:, :], rows[:, c * BANK:(c + 1) * BANK],
                                      start=True, stop=True))
            pe.wait_ge(a_done, A_P)
            if alone:
                pe.wait_ge(tables_in, 16)
            b = claim("a")
            for g in range(NG):
                for s in range(sources):
                    lo = C_BAND + (g * NT + s) * P
                    ins = pe.matmul(b[:, g * P:(g + 1) * P], p_sb[:, s * AW + g * P:s * AW + (g + 1) * P],
                                    cst[:, bass.ds(tile * (NG * NT * P) + lo, P)],
                                    start=(s == 0), stop=(s == sources - 1))
            filled("a", ins)

            pe.wait_ge(a_done, A_K)
            for heads in HEAD_PAIRS:
                b = claim("v")
                for m, hd in enumerate(heads):
                    o, c = (hd % 2) * DH, hd // 2
                    ins = pe.matmul(b[:, m * S:m * S + sources * P], qT[o:o + DH, c, :],
                                    kT[o:o + DH, c, 0:sources * P],
                                    start=True, stop=True)
                filled("v", ins)
            rows_by(C_GATE, "a")
            rows_by(C_GATE + 2, "a")
            pe.wait_ge(soft_done, HEADS)
            for hd in range(0, HEADS, 2):
                b = claim("a")
                for m in range(2):
                    for s in range(sources):
                        ins = pe.transpose(b[:, m * S + s * P:m * S + (s + 1) * P],
                                           soft[:, hd + m, s * P:(s + 1) * P], ident)
                filled("a", ins)
            rows_by(C_GATE + 4, "a")
            pe.wait_ge(a_done, A_SOFT)
            b = claim("a")
            for hd in range(HEADS):
                o, c = (hd % 2) * DH, hd // 2
                for s in range(sources):
                    ins = pe.matmul(b[o:o + DH, c * P:(c + 1) * P],
                                    v_sb[:, s * AW + hd * DH:s * AW + (hd + 1) * DH],
                                    softT[:, hd, s * P:(s + 1) * P], start=(s == 0), stop=(s == sources - 1))
            filled("a", ins)
            rows_by(C_GATE + 6, "a")

            pe.wait_ge(a_done, A_POOL)
            for g in range(0, NG, 2):
                b = claim("v")
                for m in range(2):
                    ins = pe.matmul(b[:, m * GOUT:(m + 1) * GOUT], mT[:, g + m, :], wpool[:, g + m, :],
                                    start=True, stop=True)
                filled("v", ins)

            pe.wait_ge(a_done, A_O)
            for n in range(UP_CHUNKS):
                w, b = weights(C_UP + n, UPW), claim("v")
                for c in range(NA):
                    ins = pe.matmul(b[:, :], oT[:, c, :], w[:, c, :], start=(c == 0), stop=(c == NA - 1))
                filled("v", ins)
                through(C_UP + n)
            pe.wait_ge(merged_done, 2)
            turn(lambda k: hn[:, k * P:(k + 1) * P], KC)
            pe.wait_ge(a_done, A_MERGED)
            for c in range(C_OUT, C_PQ, 2):
                rows_by(c, "v")

            pe.wait_ge(hn_done, 2)
            turn(lambda k: hn[:, k * P:(k + 1) * P], KC)
            pe.wait_ge(a_done, A_H2)
            for n in range(5):
                if n < 4:
                    cols_by(C_PQ + 2 * n)
                if n >= 1:
                    a = 4 * (n - 1)
                    pe.wait_ge(a_done, A_PQ[n - 1])
                    b = claim("a")
                    for m in range(4):
                        ins = pe.matmul(b[:, m * NK:(m + 1) * NK], pqT[:, a + m, :], keysT[:, (a + m) % 2, :],
                                        start=True, stop=True)
                    filled("a", ins)
            assert count["a"] == A_ALL

        def vector_side(dve):
            steps = [0]

            def step(ins):
                ins.then_inc(dve_step, 1)
                steps[0] += 1

            def settle():
                dve.wait_ge(dve_step, steps[0])

            return step, settle

        def mix_vector(dve, tile, window, step, settle, width=S):
            job = [0]

            def bank():
                dve.wait_ge(v_full, job[0] + 1)
                return vbank[job[0] % 4]

            def emptied(ins):
                ins.then_inc(v_done, 1)
                job[0] += 1

            def norm(n):
                dve.wait_ge(ssq_done, n + 1)
                step(dve.tensor_scalar(stat[:, 1:2], stat[:, 0:1], 1.0 / D, EPS, ALU.mult, ALU.add))
                settle()
                dve.reciprocal(stat[:, 1:2], stat[:, 1:2]).then_inc(rinv_done, 1)

            def first_norm():
                norm(0)

            def scores():
                for heads in HEAD_PAIRS:
                    b = bank()
                    for m, hd in enumerate(heads):
                        slope = 2.0 ** (-8.0 * (hd + 1) / HEADS)
                        ins = dve.scalar_tensor_tensor(
                            out=soft[:, hd, 0:width], in0=cst[:, bass.ds(tile * S + C_DIST, width)], scalar=slope,
                            in1=b[:, m * S:m * S + width], op0=ALU.mult, op1=ALU.add)
                    emptied(ins)
                    dve.wait_ge(v_done, job[0])
                    for hd in heads:
                        dve.tensor_reduce(smax[:, hd:hd + 1], soft[:, hd, 0:width], AX.X, ALU.max,
                                          negate=True).then_inc(smax_done, 1)

            def sums():
                dve.wait_ge(exp_done, HEADS)
                dve.reciprocal(srec[:, :], ssum[:, :]).then_inc(srec_done, 1)

            def branch_a():
                dve.wait_ge(a_done, A_WIDE)
                for n in range(2):
                    cols = slice(n * BANK, (n + 1) * BANK)
                    emptied(dve.tensor_tensor(hn[:, cols], bank()[:, :], pscale[:, cols], ALU.mult))
                dve.wait_ge(v_done, job[0])
                dve.wait_ge(a_done, A_GATE_A)
                step(dve.tensor_tensor(hn[:, :], hn[:, :], gates[:, 0:D], ALU.mult))

            def branch_b():
                dve.wait_ge(a_done, A_GATE_B)
                for n in range(2):
                    cols = slice(n * BANK, (n + 1) * BANK)
                    emptied(dve.tensor_tensor(tmp[:, cols], bank()[:, :],
                                              gates[:, D + n * BANK:D + (n + 1) * BANK], ALU.mult))
                    dve.wait_ge(v_done, job[0])
                    dve.tensor_tensor(hn[:, cols], hn[:, cols], tmp[:, cols], ALU.add).then_inc(merged_done, 1)

            def residual():
                for n in range(2):
                    part = xs[:, bass.ds(tile * D + n * BANK, BANK)]
                    dve.tensor_tensor(part, part, bank()[:, :], ALU.add).then_inc(x_mixed, 1)
                    job[0] += 1
                norm(1)

            def gained():
                step(dve.tensor_copy(base[:, :], cst[:, bass.ds(window + C_BASE, 1)]))
                dve.wait_ge(a_done, A_H2)
                step(dve.tensor_tensor(hn[:, :], hn[:, :], gffn, ALU.mult))

            def search(vals, idxs, data, rows):
                for lo in (0, 8):
                    if lo:
                        for r in rows:
                            step(dve.match_replace(data(r), vals(r)[:, 0:8], data(r), LOWEST))
                        settle()
                    for r in rows:
                        step(dve.max(vals(r)[:, lo:lo + 8], data(r)))
                    settle()
                    for r in rows:
                        step(dve.max_index(idxs(r)[:, lo:lo + 8], vals(r)[:, lo:lo + 8], data(r)))
                    settle()

            def key_search(n):
                dve.wait_ge(a_done, A_SCORE[n])
                search(lambda r: sv[:, r, :], lambda r: si[:, r, :], lambda r: score[:, r, :],
                       range(4 * n, 4 * n + 4))

            HH, KK = PH // 2, HK // 2

            def sum_search(half):
                heads = slice(half * HH, (half + 1) * HH)
                halves = sv[:, :, :].rearrange("p (h a) i -> p h a i", a=2)[:, heads]
                sums = cand[:, heads, :].rearrange("p h (i j) -> p h i j", i=TOPK)
                first = halves[:, :, 0, :].unsqueeze(3).to_broadcast([P, HH, TOPK, TOPK])
                second = halves[:, :, 1, :].unsqueeze(2).to_broadcast([P, HH, TOPK, TOPK])
                step(dve.tensor_tensor(sums, first, second, ALU.add))
                step(dve.tensor_copy(sif[:, 2 * half * HH:2 * (half + 1) * HH, :],
                                     si[:, 2 * half * HH:2 * (half + 1) * HH, :]))
                settle()
                search(lambda r: cv[:, r, :], lambda r: ci[:, r * TOPK:(r + 1) * TOPK],
                       lambda r: cand[:, r, :], range(half * HH, (half + 1) * HH))
                cols = slice(half * KK, (half + 1) * KK)
                step(dve.tensor_scalar(cab[:, 0, cols], ci[:, cols], 4, None, ALU.logical_shift_right))
                step(dve.tensor_scalar(cab[:, 1, cols], ci[:, cols], TOPK - 1, None, ALU.bitwise_and))
                settle()
                step(dve.tensor_copy(cabf[:, :, cols], cab[:, :, cols]))
                settle()

            def pick(half):
                cols, heads = slice(half * KK, (half + 1) * KK), slice(half * HH, (half + 1) * HH)
                hot = cand[:, heads, :].rearrange("p h (k i) -> p (h k) i", i=TOPK)
                hot4 = cand[:, heads, :].rearrange("p h (k i) -> p h k i", i=TOPK)
                ids = sif[:, :, :].rearrange("p (h a) i -> p h a i", a=2)[:, heads]
                for a in range(2):
                    step(dve.tensor_tensor(hot, cabf[:, a, cols].unsqueeze(2).to_broadcast([P, KK, TOPK]),
                                           iota16.unsqueeze(1).to_broadcast([P, KK, TOPK]), ALU.is_equal))
                    settle()
                    step(dve.tensor_tensor(hot4, hot4,
                                           ids[:, :, a, :].unsqueeze(2).to_broadcast([P, HH, TOPK, TOPK]),
                                           ALU.mult))
                    settle()
                    step(dve.tensor_reduce(picked[:, a, cols], hot, AX.X, ALU.add))
                    settle()
                step(dve.scalar_tensor_tensor(out=picked[:, 0, cols], in0=picked[:, 0, cols], scalar=float(NK),
                                              in1=picked[:, 1, cols], op0=ALU.mult, op1=ALU.add))
                settle()
                dve.tensor_scalar(expert[:, cols], picked[:, 0, cols], base[:, 0:1], None,
                                  ALU.add).then_inc(expert_ready, 1)
                dve.wait_ge(expert_ready, half + 1)

            def keys_a():
                key_search(0)
                key_search(1)

            def sums_a():
                sum_search(0)

            def pick_a():
                pick(0)

            def keys_b():
                key_search(2)
                key_search(3)

            def sums_b():
                sum_search(1)
                p3 = prob[:, :].rearrange("p (h k) -> p h k", h=PH)
                dve.tensor_tensor(p3, cv[:, :, :], cv[:, :, 0:1].to_broadcast([P, PH, TOPK]),
                                  ALU.subtract).then_inc(top_shift, 1)

            def pick_b():
                pick(1)
                dve.wait_ge(top_exp, 1)
                p3 = prob[:, :].rearrange("p (h k) -> p h k", h=PH)
                step(dve.tensor_reduce(gsum[:, :], p3, AX.X, ALU.add))
                settle()
                step(dve.reciprocal(gsum[:, :], gsum[:, :]))
                settle()
                step(dve.tensor_tensor(p3, p3, gsum[:, :].unsqueeze(2).to_broadcast([P, PH, TOPK]), ALU.mult))

            pieces = (first_norm, scores, sums, branch_a, branch_b, residual, gained, keys_a, sums_a, pick_a,
                      keys_b, sums_b, pick_b)
            return {f.__name__: f for f in pieces}


        def half_ring(pool, rows, half, source, nth):
            pool.tensor_copy(stage[:, half, :], source).then_inc(staged, 1)
            pool.wait_ge(staged, nth)
            pool.sem_inc(stage_seen, 1)
            for r in range(HALF):
                pool.indirect_dma_start(
                    ring[:, half * HALF + r, :], None, rows,
                    bass.IndirectOffsetOnAxis(ap=stage[:, half, r:r + 1], axis=0)
                ).then_inc(row_landed[half * HALF + r], 16)

        def gather_head(pool, after):
            pool.wait_ge(expert_ready, 1)
            for half in range(2):
                if after:
                    pool.wait_ge(v_step, (2 * TRIPS - 1 + half) * DVE_HALF)
                    pool.wait_ge(v_summed, (2 * TRIPS - 1 + half) * PE_HALF)
                half_ring(pool, table_rows[0], half, expert[:, half * HALF:(half + 1) * HALF],
                          after + half + 1)

        def gather_pool(pool):
            pool.tensor_copy(expert_g[:, :], expert[:, :]).then_inc(expert_taken, 1)
            pool.wait_ge(expert_taken, 1)
            with pool.Fori(0, TRIPS - 1) as i:
                for half in range(2):
                    pool.wait_ge(u_step, i * RING + (half + 1) * HALF)
                    half_ring(pool, table_rows[0], half, expert_g[:, bass.ds(i * RING + (RING + half * HALF), HALF)],
                              i * 2 + (half + 1))
            for half in range(2):
                pool.wait_ge(u_step, HK - RING + (half + 1) * HALF)
                half_ring(pool, table_rows[1], half, expert_g[:, half * HALF:(half + 1) * HALF],
                          2 * TRIPS - 2 + half + 1)
            with pool.Fori(0, TRIPS - 1) as i:
                for half in range(2):
                    pool.wait_ge(v_step, i * (2 * DVE_HALF) + (half + 1) * DVE_HALF)
                    pool.wait_ge(v_summed, i * (2 * PE_HALF) + (half + 1) * PE_HALF)
                    half_ring(pool, table_rows[1], half, expert_g[:, bass.ds(i * RING + (RING + half * HALF), HALF)],
                              i * 2 + (2 * TRIPS + half + 1))

        def gather_tanh(act):
            act.wait_ge(gelu_in, 1)
            act.activation(g2[:, :], g1[:, :], ACT.Tanh, scale=(2.0 / np.pi) ** 0.5).then_inc(tanh_done, 1)

        def diag_trip(act, n, first=False):
            if first:
                act.wait_ge(wgt_done, 1)
            for q, slot in enumerate(PE_SLOTS):
                if not (first and q < DIAGS):
                    act.wait_ge(v_summed, n * len(PE_SLOTS) + (q - DIAGS + 1))
                act.activation(diag[:, q % DIAGS, :], ident, ACT.Copy,
                               scale=wgt[:, bass.ds(n * RING + slot, 1)]).then_inc(diag_done, 1)

        def gather_tensor(pe, window):
            def trip(n, first=False, last=False):
                for q, slot in enumerate(PE_SLOTS):
                    pe.wait_ge(diag_done, n * len(PE_SLOTS) + (q + 1))
                    pe.wait_ge(row_landed[slot], window * (16 * 2 * TRIPS) + n * 16 + (TRIPS * 16 + 16))
                    for m in range(2):
                        ins = pe.matmul(vbank[2 + m][:, :], diag[:, q % DIAGS, :],
                                        ring[:, slot, m * BANK:(m + 1) * BANK],
                                        start=first and q == 0, stop=last and q == len(PE_SLOTS) - 1)
                    ins.then_inc(v_summed, 1)

            trip(0, first=True)
            with pe.Fori(1, TRIPS - 1) as n:
                trip(n)
            trip(TRIPS - 1, last=True)

        def gather_vector(dve, tile, window, step, settle):
            def landed(trip, slot):
                dve.wait_ge(row_landed[slot], window * (16 * 2 * TRIPS) + trip * 16 + 16)

            def hand_over():
                dve.tensor_copy(tok[:, :], hn[:, :]).then_inc(handed, 1)
                dve.tensor_copy(prob_g[:, :], prob[:, :]).then_inc(handed, 1)
                dve.wait_ge(handed, 2)

            def u_trip(n):
                for slot in range(RING):
                    landed(n, slot)
                    dve.scalar_tensor_tensor(
                        out=ring[:, slot, :], in0=ring[:, slot, :], scalar=1.0, in1=tok[:, :],
                        op0=ALU.mult, op1=ALU.mult,
                        accum_out=dots[:, bass.ds(n * RING + slot, 1)]).then_inc(u_step, 1)

            def weigh():
                dve.wait_ge(u_step, HK)
                step(dve.tensor_tensor(g1[:, :], dots[:, :], dots[:, :], ALU.mult))
                settle()
                step(dve.tensor_scalar(g1[:, :], g1[:, :], 0.044715, 1.0, ALU.mult, ALU.add))
                settle()
                dve.tensor_tensor(g1[:, :], g1[:, :], dots[:, :], ALU.mult).then_inc(gelu_in, 1)
                step(dve.scalar_tensor_tensor(out=wgt[:, :], in0=dots[:, :], scalar=0.5, in1=prob_g[:, :],
                                              op0=ALU.mult, op1=ALU.mult))
                step(dve.memset(acc[:, :], 0.0))
                settle()
                dve.wait_ge(tanh_done, 1)
                dve.scalar_tensor_tensor(out=wgt[:, :], in0=g2[:, :], scalar=1.0, in1=wgt[:, :],
                                         op0=ALU.add, op1=ALU.mult).then_inc(wgt_done, 1)
                dve.wait_ge(wgt_done, 1)

            def v_trip(n, first):
                for q, slot in enumerate(DVE_SLOTS):
                    landed(n + TRIPS, slot)
                    if not (first and q < 2):
                        dve.wait_ge(v_step, n * len(DVE_SLOTS) + (q - 1))
                    total = x_of(tile) if q % 2 == 0 else acc[:, :]
                    dve.scalar_tensor_tensor(out=total, in0=ring[:, slot, :],
                                             scalar=wgt[:, bass.ds(n * RING + slot, 1)], in1=total,
                                             op0=ALU.mult, op1=ALU.add).then_inc(v_step, 1)

            def close():
                dve.wait_ge(v_step, TRIPS * len(DVE_SLOTS))
                step(dve.tensor_tensor(x_of(tile), x_of(tile), acc[:, :], ALU.add))
                settle()
                dve.wait_ge(v_summed, TRIPS * len(PE_SLOTS))
                for m in range(2):
                    part = xs[:, bass.ds(tile * D + m * BANK, BANK)]
                    dve.tensor_tensor(part, part, vbank[2 + m][:, :], ALU.add).then_inc(x_final, 1)

            return hand_over, u_trip, weigh, v_trip, close

        def clear_all():
            numbers = [s.num for s in sems]
            assert numbers == list(range(numbers[0], numbers[0] + len(sems)))
            nc.sync.sem_clear(range(numbers[0], numbers[-1] + 1))
            nc.all_engine_barrier(sem_only=True)

        with nc.Block(no_gpsimd_drain=True) as block:
            @block.sync
            def _(sp):
                sp.dma_start(xs[:, 0:D], x[0, 0:P, :]).then_inc(x_in, 16)
                sp.dma_start(cst[:, 0:C_DIST], consts[:, 0:C_DIST]).then_inc(start_in, 16)

                gains_and_keys(sp, 0, first_in)
                for c in range(W_SLOTS):
                    chunk(sp, 0, c, first_w_in[c])
                sp.dma_start(cst[:, C_DIST:], consts[:, C_DIST:]).then_inc(tables_in, 16)
                sp.dma_start(xs[:, D:].rearrange("p (t d) -> p t d", d=D),
                             x[0, P:, :].rearrange("(t p) d -> p t d", p=P)).then_inc(x_rest_in, 16)
                mix_sync(sp, 0)
                sync_head(sp, 1 // NT)
                sp.wait_ge(x_rest_in, 16)

            @block.gpsimd
            def _(pool):
                gather_head(pool, 0)

            @block.scalar
            def _(act):
                mix_scalar(act, 0, lambda: act.wait_ge(x_in, 16), lambda: None, lambda: None, width=P)

            @block.tensor
            def _(pe):
                pe.wait_ge(start_in, 16)
                pe.wait_ge(cleared, 1)
                mix_tensor(pe, 0, alone=True)

            @block.vector
            def _(dve):
                dve.memset(ones[:, :], 1.0).then_inc(cleared, 1)
                dve.wait_ge(start_in, 16)
                dve.wait_ge(x_in, 16)
                step, settle = vector_side(dve)
                for name, piece in mix_vector(dve, 0, 0, step, settle, width=P).items():
                    if name == "scores":
                        dve.wait_ge(tables_in, 16)
                    piece()
                    settle()
        clear_all()

        def gather_and_mix(w, more):
            mix_tile, mix_layer = (w + 1) % NT, (w + 1) // NT
            block_of_window = nc.Block(no_gpsimd_drain=True)
            block = block_of_window.__enter__()

            @block.sync
            def _(sp):
                mix_sync(sp, mix_layer)
                if more:
                    sync_head(sp, (w + 2) // NT)

            @block.gpsimd
            def _(pool):
                gather_pool(pool)
                gather_head(pool, 4 * TRIPS - 2)

            @block.scalar
            def _(act):
                def early():
                    gather_tanh(act)
                    diag_trip(act, 0, True)
                    with act.Fori(1, TRIPS - 2) as n:
                        diag_trip(act, n)

                def late():
                    with act.Fori(TRIPS - 2, TRIPS) as n:
                        diag_trip(act, n)

                mix_scalar(act, mix_tile, lambda: act.wait_ge(handed, 2), early, late)

            @block.tensor
            def _(pe):
                mix_tensor(pe, mix_tile)
                pe.wait_ge(v_done, V_BRANCHES)
                gather_tensor(pe, w)

            @block.vector
            def _(dve):
                step, settle = vector_side(dve)
                hand_over, u_trip, weigh, v_trip, close = gather_vector(dve, w % NT, w, step, settle)
                pieces = mix_vector(dve, mix_tile, w + 1, step, settle)

                def piece(name):
                    pieces[name]()
                    settle()

                hand_over()
                piece("first_norm")
                dve.wait_ge(expert_taken, 1)
                for n, after in enumerate((None, None, "scores", "sums", "branch_a", "branch_b", "residual",
                                           "gained")):
                    u_trip(n)
                    if after:
                        piece(after)
                weigh()
                for n, after in enumerate(("keys_a", "sums_a", "pick_a", "keys_b", "sums_b", "pick_b",
                                           None, None)):
                    v_trip(n, n == 0)
                    if after:
                        piece(after)
                close()

            block_of_window.__exit__(None, None, None)
            clear_all()

        with nc.Fori(0, windows - 2) as w:
            gather_and_mix(w, True)
        gather_and_mix(windows - 2, False)

        last = windows - 1
        with nc.Block(no_gpsimd_drain=True) as block:
            def normed(t):
                return buf3[:, t * D:(t + 1) * D]

            def final_norm_scalar(act, t):
                act.activation(gates[:, 0:D], x_of(t), ACT.Square, accum_out=stat[:, 0:1]).then_inc(ssq_done, 1)
                act.wait_ge(rinv_done, t + 1)
                act.activation(stat[:, 2:3], stat[:, 1:2], ACT.Sqrt).then_inc(root_done, 1)

            @block.sync
            def _(sp):
                sp.dma_start(gffn, final_norm.unsqueeze(0).to_broadcast([P, D])).then_inc(small_in, 16)
                for t in range(NT):
                    sp.wait_ge(hn_done, t + 1)
                    sp.dma_start(out[0, t * P:(t + 1) * P, :], normed(t)).then_inc(out_in, 16)
                sp.wait_ge(out_in, 16 * NT)

            @block.gpsimd
            def _(pool):
                gather_pool(pool)

            @block.scalar
            def _(act):
                final_norm_scalar(act, 0)
                gather_tanh(act)
                diag_trip(act, 0, True)
                with act.Fori(1, TRIPS) as n:
                    diag_trip(act, n)
                act.wait_ge(x_final, 2)
                final_norm_scalar(act, 1)

            @block.tensor
            def _(pe):
                gather_tensor(pe, last)

            @block.vector
            def _(dve):
                step, settle = vector_side(dve)
                hand_over, u_trip, weigh, v_trip, close = gather_vector(dve, NT - 1, last, step, settle)

                def norm(t):
                    dve.wait_ge(ssq_done, t + 1)
                    step(dve.tensor_scalar(stat[:, 1:2], stat[:, 0:1], 1.0 / D, EPS, ALU.mult, ALU.add))
                    settle()
                    dve.reciprocal(stat[:, 1:2], stat[:, 1:2]).then_inc(rinv_done, 1)
                    dve.wait_ge(root_done, t + 1)
                    dve.scalar_tensor_tensor(out=normed(t), in0=x_of(t), scalar=stat[:, 2:3], in1=gffn,
                                             op0=ALU.mult, op1=ALU.mult).then_inc(hn_done, 1)

                hand_over()
                dve.wait_ge(small_in, 16)
                norm(0)
                with dve.Fori(0, TRIPS) as n:
                    u_trip(n)
                weigh()
                v_trip(0, True)
                with dve.Fori(1, TRIPS) as n:
                    v_trip(n, False)
                close()
                norm(1)


_INS = ["x", "mix_norm", "w_in", "w_pool", "pool_scale", "w_attn_up", "w_out", "ffn_norm", "peer_wq",
        "peer_keys", "peer_u", "peer_v", "final_norm"]


def kernel(**inputs):
    import concourse.bacc as bacc
    from concourse.bass_utils import run_bass_kernel_spmd

    nc = bacc.Bacc("TRN2", target_bir_lowering=False, num_devices=1)
    arrays, args = {}, []
    for name, a in [("consts", constants(inputs["mix_norm"].shape[0]))] + [(n, inputs[n]) for n in _INS]:
        a = np.ascontiguousarray(a)
        arrays[f"in_{name}"] = a
        args.append(nc.dram_tensor(f"in_{name}", a.shape, mybir.dt.from_np(a.dtype), kind="ExternalInput").ap())
    out = nc.dram_tensor("trunk_out", (1, S, D), F32, kind="ExternalOutput").ap()
    build(nc, *args, out)
    r = run_bass_kernel_spmd(nc, [arrays], core_ids=[0])
    return r.results[0]["trunk_out"]
```
